# Optimizing a Trainium2 kernel written in Bass

```python
import jax, jax.numpy as jnp
from jax import lax
import numpy as np

D_MODEL = 1024
BATCH = 1
SEQ = 512
DEPTH = 2

HEAD_DIM = 64
D_CONV = 512
D_LRU = 512
N_CONV_GROUPS = D_CONV // HEAD_DIM
N_LRU_HEADS = D_LRU // HEAD_DIM
D_MIX = D_CONV + D_LRU
D_IN = 3 * D_CONV + 2 * D_LRU
CONV_A_WIDTH = 3
CONV_B_WIDTH = 4
LRU_C = 8.0
D_FF = 3072
N_EXPERTS = 8
TOP_K = 2
D_FF_EXPERT = 3584
MOE_BLOCK = 128
N_DENSE = (DEPTH + 1) // 2
N_MOE = DEPTH // 2
EPS = 1e-6

kernel_name = "hymba_conv_rglru_moe_trunk"

def rms_norm(x, g):
    x32 = x.astype(jnp.float32)
    y = x32 * lax.rsqrt(jnp.mean(x32 * x32, axis=-1, keepdims=True) + EPS)
    return (y * g.astype(jnp.float32)).astype(x.dtype)

def group_rms_norm(x, g, group):
    b, s, d = x.shape
    xg = x.astype(jnp.float32).reshape(b, s, d // group, group)
    xg = xg * lax.rsqrt(jnp.mean(xg * xg, axis=-1, keepdims=True) + EPS)
    return (xg.reshape(b, s, d) * g.astype(jnp.float32)).astype(x.dtype)

def causal_depthwise_conv(u, w, bias):
    k, c = w.shape
    y = lax.conv_general_dilated(
        u, w[:, None, :].astype(u.dtype), window_strides=(1,), padding=[(k - 1, 0)],
        dimension_numbers=("NWC", "WIO", "NWC"), feature_group_count=c)
    return y + bias.astype(u.dtype)

def rg_lru(x, w_r, b_r, w_i, b_i, lam):
    b, s, d = x.shape
    x32 = x.astype(jnp.float32)
    xh = x32.reshape(b, s, N_LRU_HEADS, HEAD_DIM)
    r = jax.nn.sigmoid(jnp.einsum("bshd,hde->bshe", xh, w_r.astype(jnp.float32)).reshape(b, s, d)
                       + b_r.astype(jnp.float32))
    i = jax.nn.sigmoid(jnp.einsum("bshd,hde->bshe", xh, w_i.astype(jnp.float32)).reshape(b, s, d)
                       + b_i.astype(jnp.float32))
    log_a = -LRU_C * r * jax.nn.softplus(-lam.astype(jnp.float32))
    a = jnp.exp(log_a)
    u = jnp.sqrt(-jnp.expm1(2.0 * log_a)) * (i * x32)

    def combine(left, right):
        a1, b1 = left
        a2, b2 = right
        return a1 * a2, a2 * b1 + b2

    _, h = lax.associative_scan(combine, (a, u), axis=1)
    return h.astype(x.dtype)

def hybrid_mixer(xn, w_in, conv_a_w, conv_a_b, conv_b_w, conv_b_b,
                 w_r, b_r, w_i, b_i, lam, g_mix, w_out):
    z = jnp.einsum("bsd,de->bse", xn, w_in)
    xa, gb, gc, xr, gr = jnp.split(
        z, [D_CONV, 2 * D_CONV, 3 * D_CONV, 3 * D_CONV + D_LRU], axis=-1)
    ya = gb * causal_depthwise_conv(gc * xa, conv_a_w, conv_a_b)
    yr = rg_lru(causal_depthwise_conv(xr, conv_b_w, conv_b_b), w_r, b_r, w_i, b_i, lam) * jax.nn.gelu(gr)
    y = jnp.concatenate([ya, yr], axis=-1)
    y = group_rms_norm(y, g_mix, HEAD_DIM)
    return jnp.einsum("bse,ed->bsd", y, w_out)

def swiglu(x, w1, w3, w2):
    h = jax.nn.silu(jnp.einsum("bsd,df->bsf", x, w1)) * jnp.einsum("bsd,df->bsf", x, w3)
    return jnp.einsum("bsf,fd->bsd", h, w2)

def moe_swiglu(x, w_router, w1, w3, w2):
    b, s, d = x.shape
    t = b * s
    xf = x.reshape(t, d)
    logits = jnp.einsum("td,de->te", xf.astype(jnp.float32), w_router.astype(jnp.float32))
    top_vals, top_idx = lax.top_k(logits, TOP_K)
    gates = jax.nn.softmax(top_vals, axis=-1)
    n_assign = t * TOP_K
    expert_ids = top_idx.reshape(-1).astype(jnp.int32)
    token_ids = jnp.arange(n_assign, dtype=jnp.int32) // TOP_K
    gate_flat = gates.reshape(-1)
    order = jnp.argsort(expert_ids)
    sorted_e = expert_ids[order]
    counts = jnp.bincount(expert_ids, length=N_EXPERTS)
    padded = (counts + MOE_BLOCK - 1) // MOE_BLOCK * MOE_BLOCK
    start = jnp.cumsum(counts) - counts
    pad_end = jnp.cumsum(padded)
    pad_start = pad_end - padded
    rank = jnp.arange(n_assign, dtype=jnp.int32) - start[sorted_e]
    dest = pad_start[sorted_e] + rank
    n_blocks = -(-n_assign // MOE_BLOCK) + N_EXPERTS
    cap = n_blocks * MOE_BLOCK
    buf_tok = jnp.zeros((cap,), jnp.int32).at[dest].set(token_ids[order])
    buf_gate = jnp.zeros((cap,), jnp.float32).at[dest].set(gate_flat[order])
    block_start = jnp.arange(n_blocks, dtype=jnp.int32) * MOE_BLOCK
    block_expert = jnp.minimum(jnp.searchsorted(pad_end, block_start, side="right"), N_EXPERTS - 1)
    xb = xf[buf_tok].reshape(n_blocks, MOE_BLOCK, d)

    def expert_block(args):
        xblk, e = args
        h = jax.nn.silu(xblk @ w1[e]) * (xblk @ w3[e])
        return h @ w2[e]

    yb = lax.map(expert_block, (xb, block_expert)).reshape(cap, d)
    yb = yb * buf_gate[:, None].astype(yb.dtype)
    out = jnp.zeros((t, d), x.dtype).at[buf_tok].add(yb.astype(x.dtype))
    return out.reshape(b, s, d)

def setup_inputs(seed: int = 0) -> dict:
    key = jax.random.key(seed)
    ks = jax.random.split(key, 24)
    f32 = jnp.float32

    def nrm(k, shape, fan_in):
        return jax.random.normal(k, shape, f32) * (fan_in ** -0.5)

    def gain(k, shape):
        return 1.0 + 0.05 * jax.random.normal(k, shape, f32)

    def small(k, shape):
        return 0.02 * jax.random.normal(k, shape, f32)

    u = jax.random.uniform(ks[10], (DEPTH, D_LRU), f32, 0.9, 0.999)
    s_root = u ** (1.0 / LRU_C)
    lam = jnp.log(s_root) - jnp.log1p(-s_root)
    return {
        "x": jax.random.normal(ks[0], (BATCH, SEQ, D_MODEL), f32),
        "norm_mix_g": gain(ks[1], (DEPTH, D_MODEL)),
        "w_in": nrm(ks[2], (DEPTH, D_MODEL, D_IN), D_MODEL),
        "conv_a_w": nrm(ks[3], (DEPTH, CONV_A_WIDTH, D_CONV), CONV_A_WIDTH),
        "conv_a_b": small(ks[4], (DEPTH, D_CONV)),
        "conv_b_w": nrm(ks[5], (DEPTH, CONV_B_WIDTH, D_LRU), CONV_B_WIDTH),
        "conv_b_b": small(ks[6], (DEPTH, D_LRU)),
        "lru_w_r": nrm(ks[7], (DEPTH, N_LRU_HEADS, HEAD_DIM, HEAD_DIM), HEAD_DIM),
        "lru_b_r": small(ks[8], (DEPTH, D_LRU)),
        "lru_w_i": nrm(ks[9], (DEPTH, N_LRU_HEADS, HEAD_DIM, HEAD_DIM), HEAD_DIM),
        "lru_b_i": small(ks[11], (DEPTH, D_LRU)),
        "lru_lambda": lam,
        "mix_out_g": gain(ks[12], (DEPTH, D_MIX)),
        "w_out": nrm(ks[13], (DEPTH, D_MIX, D_MODEL), D_MIX),
        "norm_ffn_g": gain(ks[14], (DEPTH, D_MODEL)),
        "ffn_w1": nrm(ks[15], (N_DENSE, D_MODEL, D_FF), D_MODEL),
        "ffn_w3": nrm(ks[16], (N_DENSE, D_MODEL, D_FF), D_MODEL),
        "ffn_w2": nrm(ks[17], (N_DENSE, D_FF, D_MODEL), D_FF),
        "router_w": nrm(ks[18], (N_MOE, D_MODEL, N_EXPERTS), D_MODEL),
        "expert_w1": nrm(ks[19], (N_MOE, N_EXPERTS, D_MODEL, D_FF_EXPERT), D_MODEL),
        "expert_w3": nrm(ks[20], (N_MOE, N_EXPERTS, D_MODEL, D_FF_EXPERT), D_MODEL),
        "expert_w2": nrm(ks[21], (N_MOE, N_EXPERTS, D_FF_EXPERT, D_MODEL), D_FF_EXPERT),
        "final_g": gain(ks[22], (D_MODEL,)),
    }

def reference(x, norm_mix_g, w_in, conv_a_w, conv_a_b, conv_b_w, conv_b_b,
              lru_w_r, lru_b_r, lru_w_i, lru_b_i, lru_lambda, mix_out_g, w_out,
              norm_ffn_g, ffn_w1, ffn_w3, ffn_w2, router_w, expert_w1, expert_w3,
              expert_w2, final_g):
    h = x
    for layer in range(DEPTH):
        hn = rms_norm(h, norm_mix_g[layer])
        h = h + hybrid_mixer(hn, w_in[layer], conv_a_w[layer], conv_a_b[layer],
                             conv_b_w[layer], conv_b_b[layer], lru_w_r[layer], lru_b_r[layer],
                             lru_w_i[layer], lru_b_i[layer], lru_lambda[layer],
                             mix_out_g[layer], w_out[layer])
        hn = rms_norm(h, norm_ffn_g[layer])
        j = layer // 2
        if layer % 2 == 0:
            h = h + swiglu(hn, ffn_w1[j], ffn_w3[j], ffn_w2[j])
        else:
            h = h + moe_swiglu(hn, router_w[j], expert_w1[j], expert_w3[j], expert_w2[j])
    return rms_norm(h, final_g)


_drawn_inputs = setup_inputs


def setup_inputs(seed=0):
    import zlib

    import numpy as np

    out = dict(_drawn_inputs(seed))
    spreads = {}
    factors = {'lru_b_r': 4.31, 'lru_b_i': 5.647}
    for name, (base, spread) in spreads.items():
        noise = np.random.default_rng([zlib.crc32(name.encode()), seed]).standard_normal(out[name].shape)
        drawn = base * np.exp(spread * noise) if base else spread * noise
        out[name] = __import__('jax').numpy.asarray(drawn.astype(out[name].dtype))
    for name, factor in factors.items():
        out[name] = (out[name] * factor).astype(out[name].dtype)
    return out
```

```python
from contextlib import ExitStack

import concourse.bass as bass
from concourse import mybir

P = 128
F32 = mybir.dt.float32
F32R = mybir.dt.float32r
U32 = mybir.dt.uint32
I32 = mybir.dt.int32
ALU = mybir.AluOpType
ACT = mybir.ActivationFunctionType
AX = mybir.AxisListType.X

D = 1024
T = 512
KD = D // P
TB = T // P
LAYERS = 2
DC = 512
JT = DC // P
E = 8
EPS = 1e-6
RAW, CONV = 3, 6
UNIT = 2048
MIX_UNITS = 14
SECTIONS = (3, 4, 2, 0, 1)
OUT_ORDER = (0, 2, 3, 1)
FFN_G, MOE_G = 3072 // 256, 3584 // 256
HALF = T // 2
WIN = 192
MORE = (2 * T - 1) // WIN
DEEP = (T - 1) // WIN
VIS = E + MORE + 1
F0 = 2
FFN_BASE = MIX_UNITS
MIX1_BASE = FFN_BASE + 2 * 3 * FFN_G
MOE_BASE = MIX1_BASE + MIX_UNITS
MOE_F = F0 + 2 * 2 * FFN_G
BIG = 3.0e38

C_CAW, C_CAB, C_CBW, C_CBB, C_BR, C_BI, C_LAM, C_MG, C_END = 0, 24, 32, 64, 72, 80, 88, 96, 112
C_HBR, C_HBI, C_SP2 = 0, 8, 16


def build_program(nc, x, norm_mix_g, w_in, conv_a_w, conv_a_b, conv_b_w, conv_b_b, lru_w_r, lru_b_r,
                  lru_w_i, lru_b_i, lru_lambda, mix_out_g, w_out, norm_ffn_g, ffn_w1, ffn_w3, ffn_w2,
                  router_w, expert_w1, expert_w3, expert_w2, final_g, out):
    with ExitStack() as ctx:
        def sb(name, shape, dt):
            return ctx.enter_context(nc.sbuf_tensor(name, shape, dt))

        def sem(name):
            return ctx.enter_context(nc.semaphore(name))

        raw = sb("raw", [P, RAW, UNIT], F32)
        whi = sb("whi", [P, CONV, UNIT], F32R)
        wlo = sb("wlo", [P, CONV, UNIT], F32R)
        XN = sb("XN", [P, 2, KD, T], F32R)
        RES = sb("RES", [P, TB, D], F32)
        OV = sb("OV", [P, 8192], F32)
        hid = sb("hid", [P, 2, 2, HALF], F32R)
        ident = sb("ident", [P, P], F32)
        tri = sb("tri", [P, P], F32)
        ones = sb("ones", [P, P], F32)
        groups = sb("groups", [P, P], F32)
        prm = sb("prm", [P, C_END], F32)
        prm2 = sb("prm2", [P, 24], F32)
        RW = sb("RW", [P, KD, 2 * E], F32R)
        SM = sb("SM", [P, 64], F32)
        small = sb("small", [P, 8], F32)
        gates = sb("gates", [P, 2, TB], F32)
        addr = sb("addr", [P, 2, TB], U32)
        tok = sb("tok", [P, TB], U32)
        lists = sb("lists", [P, 2, VIS], U32)
        idx = sb("idx", [P, 2], U32)
        table = sb("table", [1, 8], I32)
        PS = ctx.enter_context(nc.psum_tensor("PS", [P, 8, 512], F32))

        mhalf, eps1, tiny, warm = (small[:, i:i + 1] for i in range(4))

        Y = OV[:, 0:4096].rearrange("p (t n) -> p t n", t=KD)
        xc = OV[:, 4096:5120].rearrange("p (c n) -> p c n", c=2)
        sq = OV[:, 5632:6656].rearrange("p (c n) -> p c n", c=2)
        tT, tq, tS, tu = (OV[:, 5120 + 512 * i:5632 + 512 * i] for i in range(4))
        BD = OV[:, 7168:8192].rearrange("p (g j n) -> p g j n", g=2, j=JT)
        xt = OV[:, 0:2048].rearrange("p (b n) -> p b n", b=2)
        junk = OV[:, 2048:4096].rearrange("p (b n) -> p b n", b=2)
        gB = OV[:, 4096:5120]
        prow = OV[:, 5120:5248]
        c1, s1, sl, c3, hm = (OV[:, 512 * i:512 * i + 512].rearrange("p (b n) -> p b n", b=2) for i in range(5))
        gath = OV[:, 2560:4608].rearrange("p (b n) -> p b n", b=2)
        yt = OV[:, 4608:6656].rearrange("p (b n) -> p b n", b=2)
        c1c = OV[:, 0:2048].rearrange("p (b n) -> p b n", b=2)
        gF = OV[:, 7168:8192]
        rt = [OV[:, 6656 + 32 * i:6688 + 32 * i] for i in range(16)]
        r3 = [v.rearrange("p (b e) -> p b e", b=TB) for v in rt]
        eio = r3[15]
        vec = rt[14]
        m1, i1, m2, i2, gd, zero8 = (vec[:, a:b] for a, b in ((0, 4), (4, 8), (8, 12), (12, 16), (16, 20), (24, 32)))
        extra, cum, cumx, cbase = (rt[12][:, 8 * i:8 * i + 8] for i in range(4))
        pre = OV[:, 6848:6888]
        pos = OV[:, 6912:6952]
        lamw = OV[:, 6656:6784]
        praw = OV[:, 5248:5312].rearrange("p (k e) -> p k e", k=KD)

        x_tok = nc.dram_tensor("x_tok", [T, D], F32)
        y_rows = nc.dram_tensor("y_rows", [VIS * WIN, D], F32)
        l_rows = nc.dram_tensor("l_rows", [WIN * VIS, 1], U32)

        names = """x0 x1 x2 x3 raw0 raw1 raw2 prm_in bd_in gB_in gF_in rw_in
          const_ok bd_zero step prm_T prm_ok lam_exp sp_ok rw_hi rw_ok warm_up
          ss_done mean_done rs_done xt_done xT_done xhi_done xlo_done x_stored
          hi_done lo_done z_done xc_ready gr_used gc_used xa_used gate_done tr_done ti_done T_done S_done
          yout_done sq_done stat_done rt_done yn_done yhi_done ylo_done wout_done res_done
          w1_done w3_done w2_done c1_done s1_done sl_done c3_done s3_done hm_done hh_done hl_done
          y_evac gath_in gT_done ghi_done glo_done y_stored
          log_done log_sb gd_ok gate_exp sel_ok pos_done addr_ok list_zero zero_out list_out lists_in idx_ok turns table_ok
          stream_end fin0 fin1 fin2 fin3 fin_acc fin_ready out_done""".split()
        s = {n: sem(n) for n in names}

        def lanes(v):
            return v.rearrange("(k p) n -> p k n", p=P)

        win_v = [lanes(w_in[l]) for l in range(LAYERS)]
        wout_v = [lanes(w_out[l]) for l in range(LAYERS)]
        w1_v, w3_v, w2_v = lanes(ffn_w1[0]), lanes(ffn_w3[0]), lanes(ffn_w2[0])
        e1_v, e3_v, e2_v = (w[0].rearrange("e (k p) n -> p e k n", p=P) for w in (expert_w1, expert_w3, expert_w2))
        base_of = (0, MIX1_BASE)
        Y_TILES = ((4, 5, 0, 1), (6, 7, 2, 3))
        OUT_TILES = (0, 1, 4, 5, 6, 7, 2, 3)
        done_at = {t: i for i, t in enumerate(Y_TILES[0] + Y_TILES[1])}

        def bank(i):
            return 2 * (i % 2)

        def mix_gate(eng, l, i):
            if i >= CONV:
                eng.wait_ge(s["z_done"], 10 * l + i - CONV + 1)
            elif l > 0:
                for n in ("w1_done", "w3_done", "w2_done"):
                    eng.wait_ge(s[n], MOE_F)

        def group_gate(eng, part, f, df):
            eng.wait_ge(s[("w1_done", "w3_done", "w2_done")[part]], df + (f - 2))

        block = ctx.enter_context(nc.Block())

        @block.sync
        def _(sp):
            def load(u0, du, src, parts):
                if not (isinstance(du, int) and u0 + du < RAW):
                    sp.wait_ge(s["lo_done"], du + (u0 - RAW + 1))
                sp.dma_start(raw[:, u0 % RAW, :].rearrange("p (a b) -> p a b", a=parts), src)\
                    .then_inc(s[f"raw{u0 % RAW}"], 16)

            for b in range(TB):
                sp.dma_start(RES[:, b, :], x[0, b * P:(b + 1) * P, :]).then_inc(s[f"x{b}"], 16)

            def mixer_units(l):
                for i in range(10):
                    c = SECTIONS[i % 5] * DC + (i // 5) * 256
                    load(base_of[l] + i, 0, win_v[l][:, :, c:c + 256], KD)
                for i, o in enumerate(OUT_ORDER):
                    load(base_of[l] + 10 + i, 0, wout_v[l][:, 2 * o:2 * o + 2, :], 2)

            def group(u0, du, g, a1, a3, a2):
                load(u0, du, a1(bass.ds(g * 256, 256)), KD)
                load(u0 + 1, du, a3(bass.ds(g * 256, 256)), KD)
                load(u0 + 2, du, a2(bass.ds(g * 2, 2)), 2)

            def expert_group(e, g, du):
                def of(v, a, b):
                    return v[:, bass.ds(e, 1), a, b].rearrange("p e k n -> p (e k) n")
                group(MOE_BASE, du, g, lambda c: of(e1_v, slice(0, KD), c), lambda c: of(e3_v, slice(0, KD), c),
                      lambda k: of(e2_v, k, slice(0, D)))

            mixer_units(0)
            with sp.Fori(0, 2) as h:
                with sp.Fori(0, FFN_G) as g:
                    group(FFN_BASE, h * (3 * FFN_G) + g * 3, g, lambda c: w1_v[:, :, c], lambda c: w3_v[:, :, c],
                          lambda k: w2_v[:, k, :])
            mixer_units(1)
            with sp.Fori(0, E) as v:
                with sp.Fori(0, MOE_G) as g:
                    expert_group(v, g, v * (3 * MOE_G) + g * 3)
            sp.wait_ge(s["table_ok"], 1)
            n_more = sp.value_load(table[0:1, 7:8], min_val=0, max_val=MORE)
            expert_group(sp.value_load(table[0:1, 0:1], min_val=0, max_val=E - 1), 0, E * 3 * MOE_G)
            with sp.Fori(0, MORE) as j:
                with sp.If(j < n_more):
                    e = sp.value_load(table[0:1, bass.ds(j, 1)], min_val=0, max_val=E - 1)
                    with sp.Fori(1, MOE_G) as g:
                        expert_group(e, g, j * (3 * MOE_G) + g * 3 + E * 3 * MOE_G)
                    after = sp.value_load(table[0:1, bass.ds(j + 1, 1)], min_val=0, max_val=E - 1)
                    expert_group(after, 0, j * (3 * MOE_G) + (E + 1) * 3 * MOE_G)
                with sp.Else():
                    sp.nop()
            for b in range(TB):
                sp.wait_ge(s["fin_ready"], b + 1)
                sp.dma_start(out[0, b * P:(b + 1) * P, :], RES[:, b, :]).then_inc(s["out_done"], 16)
            sp.wait_ge(s["out_done"], 16 * TB)

        @block.scalar
        def _(act):
            for n in ("c1_done", "sl_done", "c3_done", "hh_done"):
                act.sem_inc(s[n], F0)

            def split(u0, du, q):
                r = u0 % RAW
                act.wait_ge(s[f"raw{r}"], q * 16 + 16 * (u0 // RAW + 1))
                act.activation(whi[:, u0 % CONV, :], raw[:, r, :], ACT.Copy).then_inc(s["hi_done"], 1)

            def mix_split(l, i):
                mix_gate(act, l, i)
                split(base_of[l] + i, 0, 0)

            def squares(n, scratch):
                if n >= 2:
                    act.wait_ge(s["ss_done"], n - 1)
                act.activation(scratch, RES[:, n % TB, :], ACT.Square,
                               accum_out=SM[:, n:n + 1]).then_inc(s["ss_done"], 1)

            def x_hi(n):
                b = n % TB
                act.wait_ge(s["xT_done"], n + 1)
                src = PS[:, 4 + 2 * (b % 2):6 + 2 * (b % 2), :].rearrange("p a (k n) -> p (a k) n", n=P)
                act.activation(XN[:, 0, :, b * P:(b + 1) * P], src, ACT.Copy).then_inc(s["xhi_done"], 1)

            def norm(q, ready):
                for b in range(TB):
                    act.wait_ge(*ready(b))
                    squares(q * TB + b, junk[:, b % 2, :])
                    if b:
                        x_hi(q * TB + b - 1)
                x_hi(q * TB + TB - 1)

            def lru(l, jj, c):
                m = l * JT + 2 * jj + c
                act.wait_ge(s["gate_done"], m + 1)
                if c:
                    act.wait_ge(s["yout_done"], 8 * l + 4 * jj + 1)
                elif l + jj:
                    act.wait_ge(s["stat_done"], 4 * l + 2 * jj)
                act.activation(tT, PS[:, 4, :], ACT.Tanh, bias=prm2[:, C_HBR + m:C_HBR + m + 1],
                               scale=0.5).then_inc(s["tr_done"], 1)
                act.activation(tq, PS[:, 5, :], ACT.Tanh, bias=prm2[:, C_HBI + m:C_HBI + m + 1],
                               scale=0.5).then_inc(s["ti_done"], 1)
                act.wait_ge(s["tr_done"], m + 1)
                sp2 = prm2[:, C_SP2 + m:C_SP2 + m + 1]
                act.activation(tT, tT, ACT.Tanh, bias=sp2, scale=sp2).then_inc(s["T_done"], 1)
                act.wait_ge(s["T_done"], m + 1)
                act.activation(tS, tT, ACT.Sqrt, bias=tiny).then_inc(s["S_done"], 1)

            def pair_squares(l, p):
                act.wait_ge(s["yout_done"], 8 * l + 2 * p + 2)
                if l + p:
                    act.wait_ge(s["stat_done"], 4 * l + p)
                t = Y_TILES[p // 2][2 * (p % 2)]
                act.activation(sq, Y[:, t:t + 2, :], ACT.Square).then_inc(s["sq_done"], 1)

            def pair_root(l, p):
                act.wait_ge(s["stat_done"], 4 * l + p + 1)
                act.activation(PS[:, 6:8, :], PS[:, 6:8, :], ACT.Sqrt, bias=eps1).then_inc(s["rt_done"], 1)

            def y_hi(l, t):
                act.wait_ge(s["yn_done"], 8 * l + done_at[t] + 1)
                act.activation(XN[:, 0, t, :], Y[:, t, :], ACT.Copy).then_inc(s["yhi_done"], 1)

            def mixer(l):
                for jj in range(2):
                    z = 10 * l + 5 * jj
                    mix_split(l, 6 + 5 * jj)
                    if jj:
                        pair_root(l, 0)
                        pair_squares(l, 1)
                        pair_root(l, 1)
                    act.wait_ge(s["z_done"], z + 2)
                    b = bank(5 * jj + 1)
                    act.activation(Y[:, 4 + 2 * jj:6 + 2 * jj, :], PS[:, b:b + 2, :],
                                   ACT.Gelu_apprx_tanh).then_inc(s["gr_used"], 1)
                    mix_split(l, 7 + 5 * jj)
                    lru(l, jj, 0)
                    act.wait_ge(s["z_done"], z + 3)
                    b = bank(5 * jj + 2)
                    act.activation(Y[:, 2 * jj:2 * jj + 2, :], PS[:, b:b + 2, :],
                                   ACT.Copy).then_inc(s["gc_used"], 1)
                    mix_split(l, 8 + 5 * jj)
                    lru(l, jj, 1)
                    if jj == 0:
                        mix_split(l, 9)
                        mix_split(l, 10)
                        pair_squares(l, 0)
                pair_squares(l, 2)
                act.wait_ge(s["z_done"], 10 * l + 10)
                for t in (0, 1, 4, 5):
                    y_hi(l, t)
                pair_root(l, 2)
                pair_squares(l, 3)
                y_hi(l, 6)
                y_hi(l, 7)
                pair_root(l, 3)
                y_hi(l, 2)
                y_hi(l, 3)

            def hidden(u0, du, q, f0, df, n):
                def ahead(i):
                    group_gate(act, i % 3, f0 + 2 + 2 * (i // 3), df)
                    split(u0 + i, du, q)
                for i in range(4):
                    b, f = i % 2, f0 + i
                    act.wait_ge(s["w1_done"], df + (f + 1))
                    act.activation(c1[:, b, 0:n], PS[:, b, n:2 * n], ACT.Copy).then_inc(s["c1_done"], 1)
                    if b == 0:
                        ahead(3 * (i // 2))
                    act.wait_ge(s["s1_done"], df + (f + 1))
                    act.activation(sl[:, b, 0:n], s1[:, b, 0:n], ACT.Silu).then_inc(s["sl_done"], 1)
                    act.wait_ge(s["w3_done"], df + (f + 1))
                    act.activation(c3[:, b, 0:n], PS[:, 2 + b, n:2 * n], ACT.Copy).then_inc(s["c3_done"], 1)
                    if b == 1:
                        ahead(3 * (i // 2) + 1)
                    act.wait_ge(s["hm_done"], df + (f + 1))
                    act.wait_ge(s["w2_done"], df + (f - 1))
                    act.activation(hid[:, b, 0, 0:n], hm[:, b, 0:n], ACT.Copy).then_inc(s["hh_done"], 1)
                    if b == 1:
                        ahead(3 * (i // 2) + 2)

            def visit(i):
                act.wait_ge(s["gT_done"], i + 1)
                for b in range(4):
                    act.activation(XN[:, 0, 2 * b:2 * b + 2, 0:WIN],
                                   PS[:, b, 0:2 * WIN].rearrange("p (k n) -> p k n", k=2),
                                   ACT.Copy).then_inc(s["ghi_done"], 1)
                with act.Fori(0, MOE_G // 2) as g:
                    hidden(MOE_BASE + 3, i * (3 * MOE_G) + g * 6, i * MOE_G + g * 2, MOE_F,
                           i * (2 * MOE_G) + g * 4, WIN)
                act.wait_ge(s["w2_done"], i * (2 * MOE_G) + (MOE_F + 2 * MOE_G))
                act.wait_ge(s["y_stored"], i * 32 + 16)
                act.activation(yt[:, 0, :].rearrange("p (a n) -> p a n", a=2), PS[:, 4:6, :],
                               ACT.Copy).then_inc(s["y_evac"], 1)

            act.wait_ge(s["prm_ok"], 1)
            act.activation(lamw[:, 8:16], lamw[:, 0:8], ACT.Exp, scale=-1.0).then_inc(s["lam_exp"], 1)
            for i in range(2):
                mix_split(0, i)
            act.wait_ge(s["rw_in"], 16)
            act.activation(RW[:, :, 0:E], praw, ACT.Copy).then_inc(s["rw_hi"], 1)
            act.wait_ge(s["sp_ok"], 1)
            for l in range(LAYERS):
                if l:
                    act.wait_ge(s["zero_out"], 1)
                norm(2 * l, (lambda b: (s[f"x{b}"], 16)) if l == 0 else (lambda b: (s["y_evac"], 4)))
                for i in range(2 if l == 0 else 3, CONV):
                    mix_split(l, i)
                mixer(l)
                nxt = (FFN_BASE, MOE_BASE)[l]
                for i in range(2):
                    split(nxt + i, 0, 0)
                norm(2 * l + 1, lambda b: (s["res_done"], l * TB + b + 1))
                act.wait_ge(s["wout_done"], TB * (l + 1))
                split(nxt + 2, 0, 0)
                if l == 0:
                    act.activation(warm, mhalf, ACT.Silu).then_inc(s["warm_up"], 1)
                    for h in range(2):
                        with act.Fori(0, FFN_G // 2) as g:
                            hidden(FFN_BASE + 3 + h * 3 * FFN_G, g * 6, g * 2, F0 + h * 2 * FFN_G, g * 4, HALF)
            act.wait_ge(s["log_done"], 1)
            act.activation(r3[0], PS[:, 0, 0:64].rearrange("p (b e) -> p b e", b=TB)[:, :, E:2 * E],
                           ACT.Copy).then_inc(s["log_sb"], 1)
            act.wait_ge(s["gd_ok"], 1)
            act.activation(gates[:, 1, :], gd, ACT.Exp).then_inc(s["gate_exp"], 1)
            act.wait_ge(s["warm_up"], 1)
            act.activation(warm, mhalf, ACT.Silu).then_inc(s["warm_up"], 1)
            with act.Fori(0, E) as v:
                visit(v)
            act.wait_ge(s["table_ok"], 1)
            n_more = act.value_load(table[0:1, 7:8], min_val=0, max_val=MORE)
            with act.Fori(0, MORE) as j:
                with act.If(j < n_more):
                    visit(j + E)
                with act.Else():
                    act.nop()
            for b in range(TB):
                act.wait_ge(s["fin_acc"], b + 1)
                squares(4 * TB + b, c1c[:, b % 2, :])

        @block.vector
        def _(dve):
            for n in ("s1_done", "s3_done", "hm_done", "hl_done"):
                dve.sem_inc(s[n], F0)
            steps = [0]

            def step(ins):
                steps[0] += 1
                ins.then_inc(s["step"], 1)
                dve.wait_ge(s["step"], steps[0])

            def split(u0, du):
                dve.wait_ge(s["hi_done"], du + (u0 + 1))
                w = u0 % CONV
                dve.tensor_tensor(wlo[:, w, :], raw[:, u0 % RAW, :], whi[:, w, :].bitcast(F32),
                                  ALU.subtract).then_inc(s["lo_done"], 1)

            def mix_split(l, i):
                mix_gate(dve, l, i)
                split(base_of[l] + i, 0)

            def mean(n):
                dve.wait_ge(s["ss_done"], n + 1)
                dve.tensor_scalar(SM[:, 20 + n:21 + n], SM[:, n:n + 1], 1.0 / D, EPS, ALU.mult,
                                  ALU.add).then_inc(s["mean_done"], 1)

            def x_lo(n):
                b = n % TB
                dve.wait_ge(s["xhi_done"], n + 1)
                src = PS[:, 4 + 2 * (b % 2):6 + 2 * (b % 2), :].rearrange("p a (k n) -> p (a k) n", n=P)
                cols = slice(b * P, (b + 1) * P)
                dve.tensor_tensor(XN[:, 1, :, cols], src, XN[:, 0, :, cols].bitcast(F32),
                                  ALU.subtract).then_inc(s["xlo_done"], 1)

            def norm(q, add):
                for b in range(TB):
                    n = q * TB + b
                    if add:
                        add(b)
                    mean(n)
                    if b == 0:
                        dve.wait_ge(s["gB_in"], 16 * (q + 1))
                    if b >= 2:
                        dve.wait_ge(s["xT_done"], n - 1)
                        if q == 3:
                            dve.wait_ge(s["x_stored"], 16 * (b - 1))
                    dve.wait_ge(s["rs_done"], n + 1)
                    dve.scalar_tensor_tensor(xt[:, b % 2, :], RES[:, b, :], SM[:, 40 + n:41 + n], gB, ALU.mult,
                                             ALU.mult).then_inc(s["xt_done"], 1)
                    if b:
                        x_lo(n - 1)
                x_lo(q * TB + TB - 1)

            def conv(dst, src, w, bias, width, last):
                step(dve.tensor_scalar(dst, src, prm[:, w(width - 1):w(width - 1) + 1], prm[:, bias:bias + 1],
                                       ALU.mult, ALU.add))
                for back in range(1, width):
                    c = w(width - 1 - back)
                    ins = dve.scalar_tensor_tensor(dst[:, back:T], src[:, 0:T - back], prm[:, c:c + 1],
                                                   dst[:, back:T], ALU.mult, ALU.add)
                    if back == width - 1 and last:
                        ins.then_inc(s[last], 1)
                    else:
                        step(ins)

            def lru(l, jj, c):
                m = l * JT + 2 * jj + c
                dve.wait_ge(s["ti_done"], m + 1)
                step(dve.scalar_tensor_tensor(tq, tq, 1.0, xc[:, c, :], ALU.add, ALU.mult))
                dve.wait_ge(s["S_done"], m + 1)
                step(dve.tensor_scalar(tT, tT, 1.0, None, ALU.add))
                step(dve.reciprocal(tT, tT))
                step(dve.tensor_tensor(tq, tq, tT, ALU.mult))
                step(dve.tensor_tensor(tq, tq, tS, ALU.mult))
                step(dve.tensor_scalar(tT, tT, 2.0, -1.0, ALU.mult, ALU.add))
                step(dve.tensor_tensor_scan(tS, tT, tq, 0.0, ALU.mult, ALU.add))
                t = 4 + 2 * jj + c
                dve.wait_ge(s["gr_used"], 2 * l + jj + 1)
                dve.tensor_tensor(Y[:, t, :], tS, Y[:, t, :], ALU.mult).then_inc(s["yout_done"], 1)

            def pair_norm(l, p):
                dve.wait_ge(s["rt_done"], 4 * l + p + 1)
                step(dve.reciprocal(PS[:, 6:8, :], PS[:, 6:8, :]))
                for c in range(2):
                    t = Y_TILES[p // 2][2 * (p % 2) + c]
                    g = C_MG + 8 * l + t
                    dve.scalar_tensor_tensor(Y[:, t, :], Y[:, t, :], prm[:, g:g + 1], PS[:, 6 + c, :], ALU.mult,
                                             ALU.mult).then_inc(s["yn_done"], 1)

            def y_lo(l, t):
                dve.wait_ge(s["yhi_done"], 8 * l + OUT_TILES.index(t) + 1)
                dve.tensor_tensor(XN[:, 1, t, :], Y[:, t, :], XN[:, 0, t, :].bitcast(F32),
                                  ALU.subtract).then_inc(s["ylo_done"], 1)

            def mixer(l):
                for jj in range(2):
                    z = 10 * l + 5 * jj
                    dve.wait_ge(s["z_done"], z + 1)
                    if l + jj:
                        dve.wait_ge(s["gate_done"], 4 * l + 2 * jj)
                    for c in range(2):
                        j = 2 * jj + c
                        conv(xc[:, c, :], PS[:, bank(5 * jj) + c, :], lambda k: C_CBW + (l * 4 + k) * JT + j,
                             C_CBB + l * JT + j, 4, "xc_ready")
                    mix_split(l, 6 + 5 * jj)
                    if jj:
                        pair_norm(l, 0)
                        pair_norm(l, 1)
                    mix_split(l, 7 + 5 * jj)
                    lru(l, jj, 0)
                    mix_split(l, 8 + 5 * jj)
                    lru(l, jj, 1)
                    dve.wait_ge(s["z_done"], z + 4)
                    dve.wait_ge(s["gc_used"], 2 * l + jj + 1)
                    for c in range(2):
                        j = 2 * jj + c
                        ins = dve.tensor_tensor(tu, Y[:, j, :], PS[:, bank(5 * jj + 3) + c, :], ALU.mult)
                        if c:
                            ins.then_inc(s["xa_used"], 1)
                            dve.wait_ge(s["xa_used"], 2 * l + jj + 1)
                        else:
                            step(ins)
                        conv(Y[:, j, :], tu, lambda k: C_CAW + (l * 3 + k) * JT + j, C_CAB + l * JT + j, 3, None)
                    if jj == 0:
                        mix_split(l, 9)
                    dve.wait_ge(s["z_done"], z + 5)
                    b = bank(5 * jj + 4)
                    dve.tensor_tensor(Y[:, 2 * jj:2 * jj + 2, :], Y[:, 2 * jj:2 * jj + 2, :], PS[:, b:b + 2, :],
                                      ALU.mult).then_inc(s["yout_done"], 2)
                    if jj == 0:
                        mix_split(l, 10)
                for t in (0, 1, 4, 5):
                    y_lo(l, t)
                pair_norm(l, 2)
                y_lo(l, 6)
                y_lo(l, 7)
                pair_norm(l, 3)
                y_lo(l, 2)
                y_lo(l, 3)

            def add_mixer(l):
                def add(b):
                    dve.wait_ge(s["wout_done"], TB * l + b + 1)
                    p = 2 * (b % 2)
                    dve.tensor_tensor(RES[:, b, :].rearrange("p (a n) -> p a n", a=2),
                                      RES[:, b, :].rearrange("p (a n) -> p a n", a=2), PS[:, p:p + 2, :],
                                      ALU.add).then_inc(s["res_done"], 1)
                return add

            def hidden(u0, du, f0, df, n):
                def ahead(i):
                    group_gate(dve, i % 3, f0 + 2 + 2 * (i // 3), df)
                    split(u0 + i, du)
                for i in range(4):
                    b, f = i % 2, f0 + i
                    dve.wait_ge(s["c1_done"], df + (f + 1))
                    dve.tensor_tensor(s1[:, b, 0:n], PS[:, b, 0:n], c1[:, b, 0:n],
                                      ALU.add).then_inc(s["s1_done"], 1)
                    if b == 0:
                        ahead(3 * (i // 2))
                    dve.wait_ge(s["c3_done"], df + (f + 1))
                    dve.tensor_tensor(hm[:, b, 0:n], PS[:, 2 + b, 0:n], c3[:, b, 0:n],
                                      ALU.add).then_inc(s["s3_done"], 1)
                    dve.wait_ge(s["s3_done"], df + (f + 1))
                    dve.wait_ge(s["sl_done"], df + (f + 1))
                    dve.tensor_tensor(hm[:, b, 0:n], hm[:, b, 0:n], sl[:, b, 0:n],
                                      ALU.mult).then_inc(s["hm_done"], 1)
                    dve.wait_ge(s["hh_done"], df + (f + 1))
                    dve.tensor_tensor(hid[:, b, 1, 0:n], hm[:, b, 0:n], hid[:, b, 0, 0:n].bitcast(F32),
                                      ALU.subtract).then_inc(s["hl_done"], 1)
                    if b == 1:
                        ahead(3 * (i // 2) + 1)
                        ahead(3 * (i // 2) + 2)

            def visit(i):
                for b in range(4):
                    dve.wait_ge(s["ghi_done"], i * 4 + (b + 1))
                    dst = slice(2 * b, 2 * b + 2)
                    dve.tensor_tensor(XN[:, 1, dst, 0:WIN], PS[:, b, 0:2 * WIN].rearrange("p (k n) -> p k n", k=2),
                                      XN[:, 0, dst, 0:WIN].bitcast(F32), ALU.subtract).then_inc(s["glo_done"], 1)
                with dve.Fori(0, MOE_G // 2) as g:
                    hidden(MOE_BASE + 3, i * (3 * MOE_G) + g * 6, MOE_F, i * (2 * MOE_G) + g * 4, WIN)
                dve.wait_ge(s["w2_done"], i * (2 * MOE_G) + (MOE_F + 2 * MOE_G))
                dve.wait_ge(s["y_stored"], i * 32 + 16)
                dve.tensor_copy(yt[0:WIN - P, 1, :].rearrange("p (a n) -> p a n", a=2),
                                PS[0:WIN - P, 6:8, :]).then_inc(s["y_evac"], 1)

            dve.wait_ge(s["prm_T"], 1)
            step(dve.tensor_copy(prm[:, :], PS[:, 4, 0:C_END]))
            lam = prm[:, C_LAM:C_LAM + 8]
            dve.scalar_tensor_tensor(lamw[:, 0:8], lam, -1.0, lam, ALU.mult, ALU.max).then_inc(s["prm_ok"], 1)
            step(dve.tensor_scalar(prm2[:, 0:16], prm[:, C_BR:C_BR + 16], 0.5, None, ALU.mult))
            step(dve.tensor_scalar(lamw[:, 16:24], lam, -2.0, 0.0, ALU.mult, ALU.max))
            dve.wait_ge(s["lam_exp"], 1)
            ye, r, sx, s2, pl = (lamw[:, i:i + 8] for i in (8, 24, 32, 40, 48))
            step(dve.tensor_scalar(r, ye, 2.0, None, ALU.add))
            step(dve.reciprocal(r, r))
            step(dve.tensor_tensor(sx, ye, r, ALU.mult))
            step(dve.tensor_tensor(s2, sx, sx, ALU.mult))
            step(dve.tensor_scalar(pl, s2, 1.0 / 17, None, ALU.mult))
            for k in range(15, 1, -2):
                step(dve.scalar_tensor_tensor(pl, pl, 1.0 / k, s2, ALU.add, ALU.mult))
            step(dve.scalar_tensor_tensor(pl, pl, 1.0, sx, ALU.add, ALU.mult))
            dve.scalar_tensor_tensor(prm2[:, C_SP2:C_SP2 + 8], pl, 4.0, lamw[:, 16:24], ALU.mult,
                                     ALU.add).then_inc(s["sp_ok"], 1)
            for i in range(2):
                mix_split(0, i)
            dve.wait_ge(s["rw_hi"], 1)
            dve.tensor_tensor(RW[:, :, E:2 * E], praw, RW[:, :, 0:E].bitcast(F32),
                              ALU.subtract).then_inc(s["rw_ok"], 1)
            for l in range(LAYERS):
                norm(2 * l, None)
                for i in range(2 if l == 0 else 3, CONV):
                    mix_split(l, i)
                mixer(l)
                nxt = (FFN_BASE, MOE_BASE)[l]
                for i in range(2):
                    split(nxt + i, 0)
                norm(2 * l + 1, add_mixer(l))
                split(nxt + 2, 0)
                if l == 0:
                    for h in range(2):
                        with dve.Fori(0, FFN_G // 2) as g:
                            hidden(FFN_BASE + 3 + h * 3 * FFN_G, g * 6, F0 + h * 2 * FFN_G, g * 4, HALF)
                        dve.wait_ge(s["w2_done"], F0 + (h + 1) * 2 * FFN_G)
                        for c in range(2):
                            r = RES[:, 2 * h + c, :].rearrange("p (a n) -> p a n", a=2)
                            dve.tensor_tensor(r, r, PS[:, 4 + 2 * c:6 + 2 * c, :],
                                              ALU.add).then_inc(s["y_evac"], 1)

            def each(v):
                return v.unsqueeze(2).broadcast_to([P, TB, E])

            def every(v):
                return v.unsqueeze(1).broadcast_to([P, TB, E])

            L, eq, k1, L2, k2 = r3[1], r3[2], r3[3], r3[4], r3[5]
            dve.wait_ge(s["log_sb"], 1)
            dve.wait_ge(s["const_ok"], 2)
            step(dve.tensor_tensor(L, PS[:, 0, 0:64].rearrange("p (b e) -> p b e", b=TB)[:, :, 0:E], r3[0], ALU.add))

            def pick(v, m, i, mask):
                step(dve.tensor_reduce(m, v, AX, ALU.max))
                step(dve.tensor_tensor(eq, v, each(m), ALU.is_equal))
                step(dve.scalar_tensor_tensor(eq, eio, -float(E), eq, ALU.add, ALU.mult))
                step(dve.tensor_reduce(i, eq, AX, ALU.min))
                step(dve.scalar_tensor_tensor(mask, eio, -float(E), each(i), ALU.add, ALU.is_equal))

            pick(L, m1, i1, k1)
            step(dve.tensor_scalar(L2, k1, -2.0, 1.0, ALU.mult, ALU.add))
            step(dve.scalar_tensor_tensor(L2, L2, BIG, L, ALU.mult, ALU.min))
            pick(L2, m2, i2, k2)
            sel0 = pre[:, 0:E]
            pre3 = pre.rearrange("p (b e) -> p b e", e=E)
            step(dve.tensor_tensor(r3[10], k1, k2, ALU.add))
            step(dve.memset(sel0, 0.0))
            for b in range(TB):
                ins = dve.tensor_tensor(pre3[:, b + 1, :], pre3[:, b, :], r3[10][:, b, :], ALU.add)
                if b < TB - 1:
                    step(ins)
            ins.then_inc(s["sel_ok"], 1)
            dve.wait_ge(s["sel_ok"], 1)
            dve.tensor_tensor(gd, m2, m1, ALU.subtract).then_inc(s["gd_ok"], 1)
            step(dve.memset(zero8, 0.0))
            dve.wait_ge(s["pos_done"], 1)
            step(dve.tensor_copy(pos, PS[:, 1, 0:40]))
            rank = pos[:, 0:32].rearrange("p (b e) -> p b e", b=TB)
            count = pos[:, 32:40]
            wn, ad = r3[11], r3[13]
            step(dve.tensor_scalar(extra, count, float(WIN), None, ALU.is_gt))
            for d in range(2, DEEP + 1):
                step(dve.scalar_tensor_tensor(extra, count, float(WIN * d), extra, ALU.is_gt, ALU.add))
            step(dve.tensor_tensor_scan(cum, extra, zero8, 0.0, ALU.add, ALU.add))
            step(dve.tensor_tensor(cumx, cum, extra, ALU.subtract))
            step(dve.tensor_scalar(cumx, cumx, float(E - 1), None, ALU.add))
            step(dve.tensor_tensor(cbase, cumx, r3[15][:, 0, :], ALU.subtract))
            w1m = eq
            step(dve.tensor_scalar(w1m, rank, float(WIN), None, ALU.is_ge))
            step(dve.tensor_copy(wn, w1m))
            for d in range(2, DEEP + 1):
                step(dve.scalar_tensor_tensor(wn, rank, float(WIN * d), wn, ALU.is_ge, ALU.add))
            step(dve.tensor_tensor(ad, wn, every(cbase), ALU.add))
            step(dve.tensor_tensor(ad, ad, w1m, ALU.mult))
            step(dve.tensor_tensor(ad, ad, eio, ALU.add))
            step(dve.scalar_tensor_tensor(wn, wn, -float(WIN), rank, ALU.mult, ALU.add))
            step(dve.scalar_tensor_tensor(ad, wn, float(VIS), ad, ALU.mult, ALU.add))
            for n, k in enumerate((k1, k2)):
                step(dve.tensor_tensor(eq, ad, k, ALU.mult))
                step(dve.tensor_reduce((i1, i2)[n], eq, AX, ALU.add))
                ins = dve.tensor_copy(addr[:, n, :], (i1, i2)[n])
                if n == 0:
                    step(ins)
            ins.then_inc(s["addr_ok"], 1)
            step(dve.memset(m1, 0.0))
            ev = rt[0]
            for j in range(MORE + 1):
                step(dve.tensor_scalar(eq[:, 0, :], cum, float(j), None, ALU.is_le))
                step(dve.tensor_reduce(ev[:, j:j + 1], eq[:, 0, :], AX, ALU.add))
            step(dve.tensor_scalar(ev[:, 0:MORE + 1], ev[:, 0:MORE + 1], float(E - 1), None, ALU.min))
            step(dve.tensor_copy(ev[:, 7:8], cum[:, E - 1:E]))
            if MORE + 1 < 7:
                step(dve.memset(ev[:, MORE + 1:7], 0.0))
            dve.tensor_copy(table[:, :], ev[0:1, 0:8]).then_inc(s["table_ok"], 1)
            dve.wait_ge(s["gate_exp"], 1)
            step(dve.tensor_scalar(gates[:, 0, :], gates[:, 1, :], 1.0, None, ALU.add))
            step(dve.reciprocal(gates[:, 0, :], gates[:, 0, :]))
            step(dve.tensor_tensor(gates[:, 1, :], gates[:, 1, :], gates[:, 0, :], ALU.mult))
            with dve.Fori(0, E) as v:
                visit(v)
            dve.wait_ge(s["table_ok"], 1)
            n_more = dve.value_load(table[0:1, 7:8], min_val=0, max_val=MORE)
            with dve.Fori(0, MORE) as j:
                with dve.If(j < n_more):
                    visit(j + E)
                with dve.Else():
                    dve.nop()
            dve.sem_inc(s["stream_end"], 1)
            dve.wait_ge(s["gF_in"], 16)
            for b in range(TB + 1):
                if b < TB:
                    g1, g2 = (raw[:, b % RAW, D * i:D * i + D] for i in range(2))
                    dve.wait_ge(s[f"fin{b}"], 32)
                    step(dve.scalar_tensor_tensor(RES[:, b, :], g1, gates[:, 0, b:b + 1], RES[:, b, :], ALU.mult,
                                                  ALU.add))
                    dve.scalar_tensor_tensor(RES[:, b, :], g2, gates[:, 1, b:b + 1], RES[:, b, :], ALU.mult,
                                             ALU.add).then_inc(s["fin_acc"], 1)
                    mean(4 * TB + b)
                if b:
                    n = 4 * TB + b - 1
                    dve.wait_ge(s["rs_done"], n + 1)
                    dve.scalar_tensor_tensor(RES[:, b - 1, :], RES[:, b - 1, :], SM[:, 40 + n:41 + n], gF, ALU.mult,
                                             ALU.mult).then_inc(s["fin_ready"], 1)

        @block.gpsimd
        def _(pool):
            def rsqrt(n):
                pool.wait_ge(s["mean_done"], n + 1)
                pool.tensor_tensor(SM[:, 40 + n:41 + n], SM[:, 20 + n:21 + n], mhalf, ALU.pow).then_inc(s["rs_done"], 1)

            def gain(q, g):
                pool.dma_start(gB, g.partition_broadcast(P)).then_inc(s["gB_in"], 16)

            def gate_weights(l):
                for n, w in enumerate((lru_w_r, lru_w_i)):
                    v = w[l].rearrange("(j two) d e -> two d j e", two=2)
                    for h in range(2):
                        pool.dma_start(BD[64 * h:64 * h + 64, n, :, 64 * h:64 * h + 64], v[h]).then_inc(s["bd_in"], 16)

            rows = ((conv_a_w.rearrange("l k (j c) -> (l k j) c", c=P), C_CAW),
                    (conv_a_b.rearrange("l (j c) -> (l j) c", c=P), C_CAB),
                    (conv_b_w.rearrange("l k (j c) -> (l k j) c", c=P), C_CBW),
                    (conv_b_b.rearrange("l (j c) -> (l j) c", c=P), C_CBB),
                    (lru_b_r.rearrange("l (j c) -> (l j) c", c=P), C_BR),
                    (lru_b_i.rearrange("l (j c) -> (l j) c", c=P), C_BI),
                    (lru_lambda.rearrange("l (j c) -> (l j) c", c=P), C_LAM),
                    (mix_out_g.rearrange("l (j c) -> (l j) c", c=P), C_MG))
            for v, c in rows:
                pool.dma_start(prow[c:c + v.shape[0], :], v).then_inc(s["prm_in"], 16)
            gain(0, norm_mix_g[0])
            pool.dma_start(praw, router_w[0].rearrange("(k p) e -> p k e", p=P)).then_inc(s["rw_in"], 16)
            k = [0]

            def made(ins):
                k[0] += 1
                ins.then_inc(s["bd_zero"], 1)

            made(pool.memset(ident[:, :], 0.0))
            made(pool.memset(tri[:, :], 1.0))
            made(pool.memset(ones[:, :], 1.0))
            made(pool.memset(groups[:, :], 0.0))
            made(pool.memset(mhalf, -0.5))
            made(pool.memset(eps1, EPS))
            made(pool.memset(tiny, 1e-30))
            made(pool.memset(BD, 0.0))
            made(pool.memset(lists[:, :, :], 0))
            made(pool.iota(tok[:, :], pattern=[[P, TB]], base=0, channel_multiplier=1))
            pool.wait_ge(s["bd_zero"], k[0])
            made(pool.affine_select(out=ident[:, :], in_=ident[:, :], compare_op=ALU.not_equal, fill=1.0, base=0,
                                    pattern=[[-1, P]], channel_multiplier=1))
            made(pool.affine_select(out=tri[:, :], in_=tri[:, :], compare_op=ALU.is_gt, fill=0.0, base=0,
                                    pattern=[[1, P]], channel_multiplier=-1))
            pool.wait_ge(s["bd_zero"], k[0])
            made(pool.memset(groups[0:64, 0:64], 1.0 / 64))
            pool.wait_ge(s["bd_zero"], k[0])
            made(pool.memset(groups[64:P, 64:P], 1.0 / 64))
            pool.wait_ge(s["bd_zero"], k[0])
            pool.sem_inc(s["const_ok"], 1)
            gate_weights(0)
            for n in range(TB):
                rsqrt(n)
            pool.wait_ge(s["yout_done"], 6)
            gain(1, norm_ffn_g[0])
            for n in range(TB, 2 * TB):
                rsqrt(n)
            pool.wait_ge(s["w1_done"], F0 + 1)
            pool.memset(gath[:, 0, :], 0.0).then_inc(s["list_zero"], 1)
            pool.wait_ge(s["list_zero"], 1)
            y_v = y_rows[:, :].rearrange("(s v) n -> s v n", v=VIS)
            l_v = l_rows[:, :].rearrange("(s v) one -> s (v one)", v=VIS)
            blocks = ((0, P), (P, WIN))
            zeros = gath[:, 0:1, :].broadcast_to([P, VIS - E, D])
            pool.dma_start(y_v[0:P, E:VIS, :], zeros).then_inc(s["y_stored"], 16)
            pool.dma_start(y_v[P:WIN, E:VIS, :], zeros[0:WIN - P]).then_inc(s["list_out"], 16)
            for a, b in blocks:
                pool.dma_start(l_v[a:b, :], gath[0:b - a, 0, 0:VIS].bitcast(U32)).then_inc(s["list_out"], 16)
            pool.wait_ge(s["xt_done"], 8)
            gain(2, norm_mix_g[1])
            pool.wait_ge(s["gate_done"], 4)
            gate_weights(1)
            pool.wait_ge(s["y_stored"], 16)
            pool.wait_ge(s["list_out"], 48)
            pool.sem_inc(s["zero_out"], 1)
            for n in range(2 * TB, 3 * TB):
                rsqrt(n)
            pool.wait_ge(s["gate_done"], 8)
            pool.dma_start(gF, final_g.partition_broadcast(P)).then_inc(s["gF_in"], 16)
            pool.wait_ge(s["yout_done"], 14)
            gain(3, norm_ffn_g[1])
            pool.wait_ge(s["yout_done"], 16)
            pool.iota(eio, pattern=[[0, TB], [1, E]], base=0, channel_multiplier=0,
                      allow_small_or_imprecise_dtypes=True).then_inc(s["const_ok"], 1)
            for b in range(TB + 1):
                if b < TB:
                    rsqrt(3 * TB + b)
                if b:
                    if b >= 2:
                        pool.wait_ge(s["x_stored"], 16 * (b - 1))
                    pool.wait_ge(s["xt_done"], 3 * TB + b)
                    pool.dma_start(x_tok[(b - 1) * P:b * P, :], xt[:, (b - 1) % 2, :]).then_inc(s["x_stored"], 16)
            pool.wait_ge(s["addr_ok"], 1)
            for n in range(2):
                for b in range(TB):
                    pool.indirect_dma_start(l_rows[:, :], bass.IndirectOffsetOnAxis(addr[:, n, b:b + 1], 0),
                                            tok[:, b:b + 1], None).then_inc(s["list_out"], 16)
            pool.wait_ge(s["list_out"], 48 + 16 * 2 * TB)
            for n, (a, b) in enumerate(blocks):
                pool.dma_start(lists[0:b - a, n, :], l_v[a:b, :]).then_inc(s["lists_in"], 16)
            pool.wait_ge(s["lists_in"], 32)
            pool.wait_ge(s["x_stored"], 16 * TB)

            def held(semaphore, value):
                pool.wait_ge(semaphore, value)
                pool.sem_inc(s["turns"], 1)

            def gather(v, first=False):
                if not first:
                    held(s["gT_done"], v)
                pool.tensor_copy(idx[:, :], lists[:, :, 0] if first else
                                 lists[:, :, bass.ds(v, 1)].rearrange("p b one -> p (b one)")
                                 ).then_inc(s["idx_ok"], 1)
                held(s["idx_ok"], 1 if first else v + 1)
                for n, (a, b) in enumerate(blocks):
                    pool.indirect_dma_start(gath[0:b - a, n, :], None, x_tok[:, :],
                                            bass.IndirectOffsetOnAxis(idx[0:b - a, n:n + 1], 0)
                                            ).then_inc(s["gath_in"], 16)

            def visit(i):
                gather(i + 1)
                held(s["y_evac"], i * 2 + 6)
                for n, (a, b) in enumerate(blocks):
                    pool.dma_start(y_v[a:b, bass.ds(i, 1), :].rearrange("s v n -> s (v n)"),
                                   yt[0:b - a, n, :]).then_inc(s["y_stored"], 16)
                held(s["y_stored"], i * 32 + 48)
                held(s["gath_in"], i * 32 + 64)

            gather(0, first=True)
            with pool.Fori(0, E) as v:
                visit(v)
            pool.wait_ge(s["table_ok"], 1)
            n_more = pool.value_load(table[0:1, 7:8], min_val=0, max_val=MORE)
            with pool.Fori(0, MORE) as j:
                with pool.If(j < n_more):
                    visit(j + E)
                with pool.Else():
                    pool.nop()
            pool.wait_ge(s["stream_end"], 1)
            for b in range(TB):
                if b >= RAW:
                    pool.wait_ge(s["fin_acc"], b - RAW + 1)
                for n in range(2):
                    pool.indirect_dma_start(raw[:, b % RAW, D * n:D * n + D], None, y_rows[:, :],
                                            bass.IndirectOffsetOnAxis(addr[:, n, b:b + 1], 0)
                                            ).then_inc(s[f"fin{b}"], 16)
            for n in range(4 * TB, 5 * TB):
                rsqrt(n)

        @block.tensor
        def _(pe):
            for n in ("w1_done", "w3_done", "w2_done"):
                pe.sem_inc(s[n], F0)

            def mm(out_, lhsT, rhs, start, stop):
                return pe.matmul(out_, lhsT, rhs, start=start, stop=stop, skip_group_check=True)

            def x_T(q, b):
                n = q * TB + b
                if b >= 2:
                    pe.wait_ge(s["xlo_done"], n - 1)
                elif q == 0:
                    pe.wait_ge(s["prm_ok"], 1)
                elif q == 2:
                    pe.wait_ge(s["y_evac"], 4)
                elif b == 0:
                    pe.wait_ge(s["ti_done"], 2 * q + 2)
                else:
                    pe.wait_ge(s["yn_done"], 4 * q + 4)
                pe.wait_ge(s["xt_done"], n + 1)
                for k in range(KD):
                    ins = pe.transpose(PS[:, 4 + 2 * (b % 2) + k // 4, (k % 4) * P:(k % 4 + 1) * P],
                                       xt[:, b % 2, k * P:(k + 1) * P], ident[:, :])
                ins.then_inc(s["xT_done"], 1)

            def z_tile(l, i, c):
                w = (base_of[l] + i) % CONV
                o = PS[:, bank(i) + c, :]
                for k in range(KD):
                    a = slice(k * 256 + c * P, k * 256 + c * P + P)
                    mm(o, whi[:, w, a], XN[:, 0, k, :], k == 0, False)
                    mm(o, whi[:, w, a], XN[:, 1, k, :], False, False)
                    ins = mm(o, wlo[:, w, a], XN[:, 0, k, :], False, k == KD - 1)
                if c:
                    ins.then_inc(s["z_done"], 1)

            def z_waits(l, i):
                pe.wait_ge(s["lo_done"], base_of[l] + i + 1)
                if i >= 2:
                    jj, sec = (i - 2) // 5, (i - 2) % 5
                    used, v = (("xc_ready", 4 * l + 2 * jj + 2), ("gr_used", 2 * l + jj + 1),
                               ("gc_used", 2 * l + jj + 1), ("xa_used", 2 * l + jj + 1),
                               ("yout_done", 8 * l + 4 * jj + 4))[sec]
                    pe.wait_ge(s[used], v)
                elif l:
                    pe.wait_ge(s["s1_done"], MOE_F)
                    pe.wait_ge(s["s3_done"], MOE_F)

            def gate_mm(l, jj, c):
                j = 2 * jj + c
                m = l * JT + j
                pe.wait_ge(s["xc_ready"], m + 1)
                if j == 0:
                    pe.wait_ge(s["bd_in"], 64 * (l + 1))
                else:
                    pe.wait_ge(s["ti_done"], m)
                mm(PS[:, 4, :], BD[:, 0, j, :], xc[:, c, :], True, True)
                mm(PS[:, 5, :], BD[:, 1, j, :], xc[:, c, :], True, True).then_inc(s["gate_done"], 1)

            def stat(l, p):
                pe.wait_ge(s["sq_done"], 4 * l + p + 1)
                if p:
                    pe.wait_ge(s["yn_done"], 8 * l + 2 * p)
                for c in range(2):
                    ins = mm(PS[:, 6 + c, :], groups[:, :], sq[:, c, :], True, True)
                ins.then_inc(s["stat_done"], 1)

            def mixer(l):
                for b in range(TB):
                    x_T(2 * l, b)
                pe.wait_ge(s["xlo_done"], 8 * l + 4)
                for i in range(10):
                    z_waits(l, i)
                    z_tile(l, i, 0)
                    if i == 6:
                        stat(l, 1)
                    z_tile(l, i, 1)
                    if i % 5 in (1, 2):
                        gate_mm(l, i // 5, i % 5 - 1)
                    if i == 5:
                        stat(l, 0)
                    if i == 9:
                        stat(l, 2)
                for b in range(TB):
                    if b == 0:
                        pe.wait_ge(s["xa_used"], 2 * l + 2)
                    elif b == 1:
                        pe.wait_ge(s["yout_done"], 8 * l + 8)
                    else:
                        pe.wait_ge(s["res_done"], 4 * l + b - 1)
                    cols = slice(b * P, b * P + P)
                    for pos, t in enumerate(OUT_TILES):
                        if b == 0:
                            pe.wait_ge(s["ylo_done"], 8 * l + pos + 1)
                            pe.wait_ge(s["lo_done"], base_of[l] + 10 + pos // 2 + 1)
                            if pos == 2:
                                stat(l, 3)
                        w = (base_of[l] + 10 + pos // 2) % CONV
                        for xs, ws in ((0, whi), (0, wlo), (1, whi)):
                            for h in range(2):
                                a = (pos % 2) * D + h * 512
                                ins = mm(PS[:, 2 * (b % 2) + h, :], XN[:, xs, t, cols], ws[:, w, a:a + 512],
                                         pos == 0 and xs == 0 and ws is whi, pos == 7 and xs == 1)
                    ins.then_inc(s["wout_done"], 1)
                    if b:
                        x_T(2 * l + 1, b - 1)
                x_T(2 * l + 1, TB - 1)

            def up(u0, du, f0, df, t, n, xo):
                b = t % 2
                for part, done, free in ((0, "w1_done", "s1_done"), (1, "w3_done", "s3_done")):
                    u = u0 + 3 * (t // 2) + part
                    if b == 0:
                        pe.wait_ge(s["lo_done"], du + (u + 1))
                    pe.wait_ge(s[free], df + (f0 + t - 1))
                    bk = 2 * part + b
                    w = u % CONV
                    for k in range(KD):
                        a = slice(k * 256 + b * P, k * 256 + b * P + P)
                        mm(PS[:, bk, 0:2 * n], whi[:, w, a], XN[:, :, k, xo:xo + n], k == 0, False)
                        ins = mm(PS[:, bk, 0:n], wlo[:, w, a], XN[:, 0, k, xo:xo + n], False, k == KD - 1)
                    ins.then_inc(s[done], 1)

            def down(u0, du, f0, df, t, blocks, first, last):
                b = t % 2
                u = u0 + 3 * (t // 2) + 2
                if b == 0:
                    pe.wait_ge(s["lo_done"], du + (u + 1))
                pe.wait_ge(s["hl_done"], df + (f0 + t + 1))
                w = u % CONV
                for n, (lo, hi) in enumerate(blocks):
                    for xs, ws in ((0, whi), (0, wlo), (1, whi)):
                        for h in range(2):
                            a = b * D + h * 512
                            ins = mm(PS[0:hi - lo, 4 + 2 * n + h, :], hid[:, b, xs, lo:hi], ws[:, w, a:a + 512],
                                     first and xs == 0 and ws is whi, last and xs == 1)
                ins.then_inc(s["w2_done"], 1)

            def channel_mixer(u0, du, f0, df, tiles, n, xo, free):
                blocks = ((0, P), (P, n))
                up(u0, du, f0, df, 0, n, xo)
                up(u0, du, f0, df, 1, n, xo)
                if free is not None:
                    pe.wait_ge(s["y_evac"], free)
                down(u0, du, f0, df, 0, blocks, True, False)
                loops = (tiles - 4) // 4
                with pe.Fori(0, loops) as it:
                    for d in range(2, 6):
                        up(u0, it * 6 + du, f0, it * 4 + df, d, n, xo)
                        down(u0, it * 6 + du, f0, it * 4 + df, d - 1, blocks, False, False)
                for t in range(4 * loops + 2, tiles):
                    up(u0, du, f0, df, t, n, xo)
                    down(u0, du, f0, df, t - 1, blocks, False, False)
                down(u0, du, f0, df, tiles - 1, blocks, False, True)

            def visit(i):
                pe.wait_ge(s["gath_in"], i * 32 + 32)
                pe.wait_ge(s["s1_done"], i * (2 * MOE_G) + MOE_F)
                pe.wait_ge(s["s3_done"], i * (2 * MOE_G) + MOE_F)
                for k in range(KD):
                    for n, (a, b) in enumerate(((0, P), (P, WIN))):
                        ins = pe.transpose(PS[:, k // 2, (k % 2) * WIN + a:(k % 2) * WIN + b],
                                           gath[0:b - a, n, k * P:(k + 1) * P], ident[0:b - a, 0:b - a])
                ins.then_inc(s["gT_done"], 1)
                pe.wait_ge(s["glo_done"], i * 4 + 4)
                channel_mixer(MOE_BASE, i * (3 * MOE_G), MOE_F, i * (2 * MOE_G), 2 * MOE_G, WIN, 0, i * 2 + 4)

            pe.wait_ge(s["prm_in"], 128)
            pe.wait_ge(s["const_ok"], 1)
            pe.transpose(PS[:, 4, 0:C_END], prow[0:C_END, :], ident[0:C_END, 0:C_END]).then_inc(s["prm_T"], 1)
            mixer(0)
            pe.wait_ge(s["xlo_done"], 8)
            for h in range(2):
                channel_mixer(FFN_BASE + h * 3 * FFN_G, 0, F0 + h * 2 * FFN_G, 0, 2 * FFN_G, HALF, h * HALF,
                              2 * h if h else None)
            mixer(1)
            pe.wait_ge(s["rw_ok"], 1)
            pe.wait_ge(s["xlo_done"], 16)
            pe.wait_ge(s["res_done"], 8)
            for b in range(TB):
                c = 2 * E * b
                for k in range(KD):
                    mm(PS[:, 0, c:c + 2 * E], XN[:, 0, k, b * P:(b + 1) * P], RW[:, k, :], k == 0, False)
                    ins = mm(PS[:, 0, c:c + E], XN[:, 1, k, b * P:(b + 1) * P], RW[:, k, 0:E], False, k == KD - 1)
            ins.then_inc(s["log_done"], 1)
            pe.wait_ge(s["sel_ok"], 1)
            mm(PS[:, 1, 0:32], tri[:, :], rt[10], True, False)
            mm(PS[:, 1, 0:32], ones[:, :], pre[:, 0:32], False, True)
            mm(PS[:, 1, 32:40], ones[:, :], pre[:, 32:40], True, True).then_inc(s["pos_done"], 1)
            with pe.Fori(0, E) as v:
                visit(v)
            pe.wait_ge(s["table_ok"], 1)
            n_more = pe.value_load(table[0:1, 7:8], min_val=0, max_val=MORE)
            with pe.Fori(0, MORE) as j:
                with pe.If(j < n_more):
                    visit(j + E)
                with pe.Else():
                    pe.nop()


_INS = ["x", "norm_mix_g", "w_in", "conv_a_w", "conv_a_b", "conv_b_w", "conv_b_b", "lru_w_r", "lru_b_r",
        "lru_w_i", "lru_b_i", "lru_lambda", "mix_out_g", "w_out", "norm_ffn_g", "ffn_w1", "ffn_w3", "ffn_w2",
        "router_w", "expert_w1", "expert_w3", "expert_w2", "final_g"]


def kernel(**inputs):
    import numpy as np
    import concourse.bacc as bacc
    from concourse.bass_utils import run_bass_kernel_spmd

    nc = bacc.Bacc("TRN2", target_bir_lowering=False, num_devices=1)
    arrays, args = {}, []
    for name in _INS:
        a = np.ascontiguousarray(inputs[name])
        arrays[f"in_{name}"] = a
        args.append(nc.dram_tensor(f"in_{name}", a.shape, mybir.dt.from_np(a.dtype), kind="ExternalInput").ap())
    args.append(nc.dram_tensor("out_0", (1, T, D), F32, kind="ExternalOutput").ap())
    build_program(nc, *args)
    r = run_bass_kernel_spmd(nc, [arrays], core_ids=[0])
    return r.results[0]["out_0"]
```
